# Optimizing a Trainium2 kernel written in Bass

```python
import jax, jax.numpy as jnp
from jax import lax
import numpy as np

D_MODEL = 1024
BATCH = 1
SEQ = 256
DEPTH = 2
DEC_BATCH = 8
DEC_SEQ = 1
PAST_LEN = 2048
PAGE_SIZE = 128

N_HEADS = 8
HEAD_K = D_MODEL // N_HEADS
HEAD_V = D_MODEL // N_HEADS
CHUNK = 32
CONV_W = 3
D_FF = 7 * D_MODEL // 2
N_EXPERTS = 8
TOP_K = 2
N_EVEN = (DEPTH + 1) // 2
N_ODD = DEPTH // 2
EPS = 1e-6

kernel_name = "hgrn2_shortconv_moe_hybrid_step"

F32 = jnp.float32

def rmsnorm(x, g):
    xf = x.astype(F32)
    y = xf * lax.rsqrt(jnp.mean(xf * xf, axis=-1, keepdims=True) + EPS) * g.astype(F32)
    return y.astype(x.dtype)

def hgrn2_features(xn, w_in, lb):
    bs, t, _ = xn.shape
    q, fl, v, gate = jnp.split(xn @ w_in, 4, axis=-1)
    q = jax.nn.silu(q.astype(F32)).reshape(bs, t, N_HEADS, HEAD_K)
    f = lb + (1.0 - lb) * jax.nn.sigmoid(fl.astype(F32))
    logf = jnp.log(f).reshape(bs, t, N_HEADS, HEAD_K)
    k = (1.0 - f).reshape(bs, t, N_HEADS, HEAD_K)
    v = v.astype(F32).reshape(bs, t, N_HEADS, HEAD_V)
    return q, k, v, logf, gate

def hgrn2_chunked(q, k, v, logf):
    bs, t = q.shape[:2]
    n = t // CHUNK

    def to_chunks(a):
        return a.reshape(bs, n, CHUNK, N_HEADS, a.shape[-1]).swapaxes(0, 1)

    G = jnp.cumsum(to_chunks(logf), axis=2)
    mask = jnp.tril(jnp.ones((CHUNK, CHUNK), dtype=bool))

    def step(S, xs):
        qc, kc, vc, Gc = xs
        g_last = Gc[:, -1]
        q_in = qc * jnp.exp(Gc)
        k_in = kc * jnp.exp(-Gc)
        A = jnp.where(mask, jnp.einsum('bthk,bshk->bhts', q_in, k_in), 0.0)
        o = jnp.einsum('bhts,bshv->bthv', A, vc) + jnp.einsum('bthk,bhkv->bthv', q_in, S)
        k_dec = kc * jnp.exp(g_last[:, None] - Gc)
        S = jnp.exp(g_last)[..., None] * S + jnp.einsum('bshk,bshv->bhkv', k_dec, vc)
        return S, o

    S0 = jnp.zeros((bs, N_HEADS, HEAD_K, HEAD_V), F32)
    S, o = lax.scan(step, S0, (to_chunks(q), to_chunks(k), to_chunks(v), G))
    o = o.swapaxes(0, 1).reshape(bs, t, N_HEADS, HEAD_V)
    return o, S

def hgrn2_recurrent(q, k, v, logf, S0):
    def step(S, xs):
        qt, kt, vt, lft = xs
        S = jnp.exp(lft)[..., None] * S + kt[..., None] * vt[..., None, :]
        return S, jnp.einsum('bhk,bhkv->bhv', qt, S)

    S, o = lax.scan(step, S0.astype(F32), tuple(a.swapaxes(0, 1) for a in (q, k, v, logf)))
    return o.swapaxes(0, 1), S

def hgrn2_out(o, gate, g_norm, w_out, dtype):
    bs, t = o.shape[:2]
    o = o * lax.rsqrt(jnp.mean(o * o, axis=-1, keepdims=True) + EPS)
    o = o.reshape(bs, t, D_MODEL) * g_norm.astype(F32) * jax.nn.silu(gate.astype(F32))
    return o.astype(dtype) @ w_out

def short_conv_mix(xn, buf, w_in, conv_w, w_out):
    b, c, h = jnp.split(xn @ w_in, 3, axis=-1)
    u = c * h
    u_ext = jnp.concatenate([buf.astype(u.dtype), u], axis=1)
    t = u.shape[1]
    y = conv_w[0] * u_ext[:, 0:t]
    for j in range(1, CONV_W):
        y = y + conv_w[j] * u_ext[:, j:j + t]
    return (b * y) @ w_out, u_ext[:, -(CONV_W - 1):]

def swiglu(x, w1, w3, w2):
    return (jax.nn.silu(x @ w1) * (x @ w3)) @ w2

def moe_swiglu(x, router, w1, w3, w2):
    bs, t, d = x.shape
    xt = x.reshape(-1, d)
    logits = (xt @ router).astype(F32)
    top_v, top_i = lax.top_k(logits, TOP_K)
    gates = jax.nn.softmax(top_v, axis=-1)
    combine = jnp.sum(jax.nn.one_hot(top_i, N_EXPERTS, dtype=F32) * gates[..., None], axis=1)
    out = jnp.zeros(xt.shape, F32)
    for e in range(N_EXPERTS):
        out = out + combine[:, e:e + 1] * swiglu(xt, w1[e], w3[e], w2[e]).astype(F32)
    return out.astype(x.dtype).reshape(bs, t, d)

def setup_inputs(seed: int = 0) -> dict:
    key = jax.random.key(seed)
    ks = jax.random.split(key, 20)
    n = lambda k, s, sc: jax.random.normal(k, s, F32) * sc
    D = D_MODEL
    return {
        "x_prompt": n(ks[0], (BATCH, SEQ, D), 1.0),
        "x_sample": n(ks[1], (DEC_BATCH, DEC_SEQ, D), 1.0),
        "state_hgrn": n(ks[2], (DEC_BATCH, N_EVEN, N_HEADS, HEAD_K, HEAD_V), 0.5),
        "state_conv": n(ks[3], (DEC_BATCH, N_ODD, CONV_W - 1, D), 1.0),
        "norm_mix": 1.0 + n(ks[4], (DEPTH, D), 0.02),
        "norm_ffn": 1.0 + n(ks[5], (DEPTH, D), 0.02),
        "norm_final": 1.0 + n(ks[6], (D,), 0.02),
        "hgrn_w_in": n(ks[7], (N_EVEN, D, 4 * D), D ** -0.5),
        "hgrn_lb": n(ks[8], (DEPTH + 1, D), 0.1),
        "hgrn_g_norm": 1.0 + n(ks[9], (N_EVEN, D), 0.02),
        "hgrn_w_out": n(ks[10], (N_EVEN, D, D), D ** -0.5),
        "conv_w_in": n(ks[11], (N_ODD, D, 3 * D), D ** -0.5),
        "conv_w": n(ks[12], (N_ODD, CONV_W, D), CONV_W ** -0.5),
        "conv_w_out": n(ks[13], (N_ODD, D, D), D ** -0.5),
        "ffn_w1": n(ks[14], (N_EVEN, D, D_FF), D ** -0.5),
        "ffn_w3": n(ks[15], (N_EVEN, D, D_FF), D ** -0.5),
        "ffn_w2": n(ks[16], (N_EVEN, D_FF, D), D_FF ** -0.5),
        "moe_router": n(ks[17], (N_ODD, D, N_EXPERTS), D ** -0.5),
        "moe_w1": n(ks[18], (N_ODD, N_EXPERTS, D, D_FF), D ** -0.5),
        "moe_w3": n(jax.random.fold_in(ks[19], 0), (N_ODD, N_EXPERTS, D, D_FF), D ** -0.5),
        "moe_w2": n(jax.random.fold_in(ks[19], 1), (N_ODD, N_EXPERTS, D_FF, D), D_FF ** -0.5),
    }

def reference(x_prompt, x_sample, state_hgrn, state_conv, norm_mix, norm_ffn, norm_final,
              hgrn_w_in, hgrn_lb, hgrn_g_norm, hgrn_w_out, conv_w_in, conv_w, conv_w_out,
              ffn_w1, ffn_w3, ffn_w2, moe_router, moe_w1, moe_w3, moe_w2):
    lb_all = jnp.cumsum(jax.nn.softmax(hgrn_lb.astype(F32), axis=0), axis=0)
    xp, xs = x_prompt, x_sample
    hgrn_p, hgrn_s, conv_p, conv_s = [], [], [], []
    for i in range(DEPTH):
        j = i // 2
        if i % 2 == 0:
            xn = rmsnorm(xp, norm_mix[i])
            q, k, v, lf, gate = hgrn2_features(xn, hgrn_w_in[j], lb_all[i])
            o, S = hgrn2_chunked(q, k, v, lf)
            xp = xp + hgrn2_out(o, gate, hgrn_g_norm[j], hgrn_w_out[j], xp.dtype)
            hgrn_p.append(S.astype(xp.dtype))

            xn = rmsnorm(xs, norm_mix[i])
            q, k, v, lf, gate = hgrn2_features(xn, hgrn_w_in[j], lb_all[i])
            o, S = hgrn2_recurrent(q, k, v, lf, state_hgrn[:, j])
            xs = xs + hgrn2_out(o, gate, hgrn_g_norm[j], hgrn_w_out[j], xs.dtype)
            hgrn_s.append(S.astype(state_hgrn.dtype))

            xp = xp + swiglu(rmsnorm(xp, norm_ffn[i]), ffn_w1[j], ffn_w3[j], ffn_w2[j])
            xs = xs + swiglu(rmsnorm(xs, norm_ffn[i]), ffn_w1[j], ffn_w3[j], ffn_w2[j])
        else:
            zero_buf = jnp.zeros((xp.shape[0], CONV_W - 1, D_MODEL), xp.dtype)
            y, buf = short_conv_mix(rmsnorm(xp, norm_mix[i]), zero_buf, conv_w_in[j], conv_w[j], conv_w_out[j])
            xp = xp + y
            conv_p.append(buf)
            y, buf = short_conv_mix(rmsnorm(xs, norm_mix[i]), state_conv[:, j], conv_w_in[j], conv_w[j], conv_w_out[j])
            xs = xs + y
            conv_s.append(buf.astype(state_conv.dtype))

            xp = xp + moe_swiglu(rmsnorm(xp, norm_ffn[i]), moe_router[j], moe_w1[j], moe_w3[j], moe_w2[j])
            xs = xs + moe_swiglu(rmsnorm(xs, norm_ffn[i]), moe_router[j], moe_w1[j], moe_w3[j], moe_w2[j])
    y_prompt = rmsnorm(xp, norm_final)
    y_sample = rmsnorm(xs, norm_final)
    state_hgrn_prompt = jnp.stack(hgrn_p, axis=1)
    state_hgrn_sample = jnp.stack(hgrn_s, axis=1)
    state_conv_prompt = jnp.stack(conv_p, axis=1)
    state_conv_sample = jnp.stack(conv_s, axis=1)
    return (y_prompt, y_sample, state_hgrn_prompt, state_hgrn_sample, state_conv_prompt, state_conv_sample)


_drawn_inputs = setup_inputs


def setup_inputs(seed=0):
    import zlib

    import numpy as np

    out = dict(_drawn_inputs(seed))
    spreads = {}
    factors = {}
    for name, (base, spread) in spreads.items():
        noise = np.random.default_rng([zlib.crc32(name.encode()), seed]).standard_normal(out[name].shape)
        drawn = base * np.exp(spread * noise) if base else spread * noise
        out[name] = __import__('jax').numpy.asarray(drawn.astype(out[name].dtype))
    for name, factor in factors.items():
        out[name] = (out[name] * factor).astype(out[name].dtype)
    return out
```

```python
from contextlib import ExitStack

import concourse.bass as bass
from concourse import mybir

ALU = mybir.AluOpType
ACT = mybir.ActivationFunctionType
AX = mybir.AxisListType
F32 = mybir.dt.float32
F32R = mybir.dt.float32r
BF16 = mybir.dt.bfloat16
I32 = mybir.dt.int32

P = 128
EPS = 1e-6
RAW = 3
SPLIT = 3
AHEAD = SPLIT - 1
SPLIT_M = 6
AHEAD_M = SPLIT_M - 1


def build(nc, x_prompt, x_sample, state_hgrn, state_conv, norm_mix, norm_ffn, norm_final,
          hgrn_w_in, hgrn_lb, hgrn_g_norm, hgrn_w_out, conv_w_in, conv_w, conv_w_out,
          ffn_w1, ffn_w3, ffn_w2, moe_router, moe_w1, moe_w3, moe_w2,
          y_prompt, y_sample, hgrn_prompt, hgrn_sample, conv_prompt, conv_sample):
    D = x_prompt.shape[2]
    TP = x_prompt.shape[1]
    B = x_sample.shape[0]
    T = TP + B
    DT = D // P
    BLK = TP // P
    TT = BLK + 1
    CH = 32
    CPB = P // CH
    NC = TP // CH
    FF = ffn_w1.shape[2]
    FW = 512
    FB = FF // FW
    E = moe_router.shape[2]
    CW = 4096
    PW = CW // 2
    rows = [P] * BLK + [B]

    C_IN, C_OUT = 0, 8
    C_FFN = C_OUT + 2
    C_CIN = C_FFN + 3 * FB
    C_COUT = C_CIN + 6
    C_MOE = C_COUT + 2
    JOB = 3 * FB
    assert C_MOE % RAW == 0 and JOB % RAW == 0 and C_FFN * 2 + 4 == 24

    def kp(w):
        return w.rearrange("(k p) n -> p k n", p=P)

    with ExitStack() as ctx:
        top = [(nc.sbuf_base + 63) // 64 * 64]

        def at(name, shape, dt, offset):
            return nc.alloc_sbuf_tensor_at(name, shape, dt, offset=offset)

        def size(shape, dt):
            n = 2 if dt == BF16 else 4
            for s in shape[1:]:
                n *= s
            return (n + 31) // 32 * 32

        def keep(name, shape, dt=F32):
            t = at(name, shape, dt, top[0])
            top[0] += size(shape, dt)
            return t

        raw = keep("raw", [P, RAW, CW])
        whi = keep("whi", [P, SPLIT, PW], F32R)
        wlo = keep("wlo", [P, SPLIT, PW], F32R)
        xT = keep("xT", [P, DT, T])
        xn = keep("xn", [P, DT, T])
        xh = keep("xh", [P, DT, T], F32R)
        xl = keep("xl", [P, DT, T], F32R)
        ident = keep("ident", [P, P])
        ones = keep("ones", [P, P])
        causal = keep("causal", [P, P])
        before = keep("before", [P, P])
        iota = keep("iota", [P, P])
        VN = {"mix0": 0, "mix1": 8, "ffn0": 16, "ffn1": 24, "final": 32, "lb0": 40, "lb1": 48,
              "lb2": 56, "gn": 64, "cw0": 72, "cw1": 80, "cw2": 88}
        NV = 96
        vecs = keep("vecs", [P, NV])
        bufT = keep("bufT", [P, DT, B, 2])
        eps = keep("eps", [P, 1])
        lbs = keep("lbs", [P, 6, DT])
        router = keep("router", [P, DT, E])
        R0 = top[0]
        assert R0 + 91000 < nc.sbuf_usable_end, (R0, nc.sbuf_usable_end)

        def region(offset, *specs):
            out = []
            for name, shape, dt in specs:
                out.append(at(name, shape, dt, offset))
                offset += size(shape, dt)
                assert offset <= nc.sbuf_usable_end, (name, offset)
            return out, offset

        (xrows, vrows, brows), _ = region(
            R0, ("xrows", [P, TT, D], F32), ("vrows", [NV, P], F32), ("brows", [2 * B, D], F32))
        (z,), Z1 = region(R0, ("z", [P, 4 * DT, T], F32))
        (kk, pa, pb), o = region(Z1, ("kk", [P, DT, T], F32), ("pa", [P, DT, T], F32),
                                 ("pb", [P, DT, T], F32))
        (vtok, ktok, amask), o = region(
            o, ("vtok", [P, BLK, 4, P], F32), ("ktok", [P, BLK, 4, P], F32),
            ("amask", [P, BLK, 4, P], F32))
        (U, plast), o = region(o, ("U", [P, NC, 4, P], F32), ("plast", [P, DT, NC], F32))
        (st,), _ = region(Z1 + size([P, DT, T], F32), ("st", [P, 2, B, P], F32))
        (ks, vs, vbd), _ = region(
            Z1 + 3 * size([P, DT, T], F32) + 3 * 4096,
            ("ks", [B, DT, P], F32), ("vs", [B, DT, P], F32), ("vbd", [B, 2, B, P], F32))
        oT = xn
        (rs4, _), _ = region(Z1, ("rs4", [P, 2, 4, T], F32), ("none", [P, 8], F32))
        N0 = Z1 + 4 * size([P, DT, T], F32)
        (sq, rs, rstd), _ = region(N0, ("sq", [P, DT, T], F32), ("rs", [P, T], F32),
                                   ("rstd", [P, T], F32))
        (fh, fl, fs, fx), _ = region(
            R0, ("fh", [P, 4, T], F32R), ("fl", [P, 4, T], F32R), ("fs", [P, 4, T], F32),
            ("fx", [P, 4, T], F32))
        UE = 2 + TP + 3 * B
        (zc, ue, yc, cg, cgr), o = region(
            R0, ("zc", [P, 2 * DT, T], F32), ("ue", [P, DT, UE], F32),
            ("yc", [P, DT, UE - 2], F32), ("cg", [P, DT, 2 + B], F32), ("cgr", [2 + B, D], F32))
        assert o <= N0
        (xtok, xgh, xgl, pm, pw, pwt, hs, hx, hth, htl, ysb, zero), o = region(
            R0, ("xtok", [P, TT, D], F32), ("xgh", [P, DT, P], F32R), ("xgl", [P, DT, P], F32R),
            ("pm", [P, TT, P], F32), ("pw", [P, TT, P], F32), ("pwt", [P, T], F32),
            ("hs", [P, FW], F32), ("hx", [P, FW], F32), ("hth", [P, 4, P], F32R),
            ("htl", [P, 4, P], F32R), ("ysb", [P, D], F32), ("zero", [P, FW], BF16))
        NS = 3 * E
        (lg, tk, oh1, oh2, sel, wt, iote, valid, ptab, cnt, flag), o = region(
            o, ("lg", [P, TT, E], F32), ("tk", [P, 10, TT], F32), ("oh1", [P, TT, E], F32),
            ("oh2", [P, TT, E], F32), ("sel", [P, TT, E], F32), ("wt", [P, TT, E], F32),
            ("iote", [P, E], F32), ("valid", [P, TT], F32), ("ptab", [P, TT, NS], F32),
            ("cnt", [P, E], F32), ("flag", [P, NS + 8], I32))
        (whi2, wlo2), o = region(o, ("whi2", [P, SPLIT_M - SPLIT, PW], F32R),
                                 ("wlo2", [P, SPLIT_M - SPLIT, PW], F32R))

        def bufs(q):
            b = q % SPLIT_M
            return (whi[:, b, :], wlo[:, b, :]) if b < SPLIT else (
                whi2[:, b - SPLIT, :], wlo2[:, b - SPLIT, :])

        (yrows,), _ = region(R0 + 45000 // 64 * 64, ("yrows", [P, TT, D], F32))

        Q = [ctx.enter_context(nc.psum_tensor(f"Q{i}", [P, 4, 512], F32)) for i in range(2)]

        sems = {}

        def sem(name):
            if name not in sems:
                sems[name] = ctx.enter_context(nc.semaphore(name))
            return sems[name]

        uses = ["x0", "x1", "vec", "ss_mix0"] + [f"in{c}" for c in range(8)]
        for g in range(2):
            uses += [f"t{g}", f"a{g}", f"d{g}0", f"d{g}1", f"o{g}"]
        uses += ["ts", "os", "outer", "on0", "on1", "out0", "out1", "ss_ffn0"]
        uses += ["ss_mix1"] + [f"cin{c}" for c in range(6)]
        uses += ["cg", "cout0", "cout1", "ss_ffn1", "lg", "xt0", "xt1", "rank", "xt2"]
        place = {n: (i % 2, i // 2) for i, n in enumerate(uses)}

        def quad(name):
            return Q[place[name][0]]

        def ss_bank(which):
            return Q[0][:, 3, :] if which == "final" else quad("ss_" + which)[:, 0, :]

        def quad_free(name):
            return sem(f"quad_free{place[name][0]}")

        def before_quad(eng, name):
            _, nth = place[name]
            if nth:
                eng.wait_ge(quad_free(name), 2 * nth)

        def let_go(name):
            return quad_free(name)

        raw_loaded = [sem(f"raw_loaded{i}") for i in range(RAW)]
        hi_done, lo_done, used = sem("hi_done"), sem("lo_done"), sem("pieces_used")

        block = ctx.enter_context(nc.Block())

        def out_state(sp, h):
            sp.wait_ge(sem("state_new"), h + 1)
            sp.wait_ge(sem("state_read"), h + 1)
            sp.dma_start(hgrn_sample[:, 0, h].rearrange("b k v -> k b v"), st[:, h % 2, :, :]
                         ).then_inc(sem("state_out"), 16)

        def jobs(eng, head, body):
            head(0, 0, 0)
            with eng.Fori(0, E - 1) as e:
                body(e, e, e, True)
            body(E - 1, E - 1, E - 1, False)
            more = eng.value_load(flag[0:1, NS:NS + 1], min_val=0, max_val=1)
            with eng.If(more > 0):
                count = eng.alloc_register("jobs_done")
                eng.reg_mov(count, E)
                with eng.Fori(1, 3) as c:
                    with eng.Fori(0, E) as e:
                        col = c * E + e
                        here = eng.value_load(flag[0:1, bass.ds(col, 1)], min_val=0, max_val=1)
                        with eng.If(here > 0):
                            k = eng.snap(count, min_val=E, max_val=3 * E)
                            head(k, e, col)
                            body(k, e, col, False)
                            eng.reg_add(count, count, 1)
                            eng.nop()
                        eng.end_ifs()
                        eng.nop()
            eng.end_ifs()

        def turn_x(t_, t, rows):
            r = rows[t]
            for d in range(DT):
                mm = t_.transpose(quad(f"xt{t}")[0:r, d // 4, P * (d % 4):P * (d % 4 + 1)],
                                  xn[:, d, P * t:P * t + r], ident[:, :])
            return mm

        @block.sync
        def _(sp):
            def chunk(n, src, slot=None):
                if slot is None:
                    slot = n % RAW
                if not isinstance(n, int) or n >= RAW:
                    sp.wait_ge(lo_done, n * 2 - (2 * RAW - 2))
                k, w = src.shape[1], src.shape[2]
                dst = raw[:, slot, :].rearrange("p (k w) -> p k w", k=k)
                sp.dma_start(dst, src).then_inc(raw_loaded[slot], 16)

            sp.dma_start(xrows[:, 0:BLK, :], x_prompt[0].rearrange("(b p) d -> p b d", p=P)
                         ).then_inc(sem("x_loaded"), 16)
            sp.dma_start(xrows[0:B, BLK, :], x_sample[:, 0, :]).then_inc(sem("x_loaded"), 16)
            for src, row in ((norm_mix, 0), (norm_ffn, 16), (norm_final, 32), (hgrn_lb, 40),
                             (hgrn_g_norm, 64), (conv_w[0], 72)):
                if len(src.shape) == 1:
                    v, n = src.rearrange("(a q) -> a q", q=P), 8
                else:
                    v, n = src.rearrange("r (a q) -> (r a) q", q=P), 8 * src.shape[0]
                sp.dma_start(vrows[row:row + n, :], v).then_inc(sem("small_loaded"), 16)
            sp.dma_start(brows[:, :], state_conv.rearrange("b o r d -> (b o r) d")
                         ).then_inc(sem("small_loaded"), 16)
            sp.dma_start(router[:, :, :], kp(moe_router[0])).then_inc(sem("small_loaded"), 16)

            for c in range(8):
                chunk(C_IN + c, kp(hgrn_w_in[0])[:, :, FW * c:FW * (c + 1)])
            for c in range(2):
                chunk(C_OUT + c, kp(hgrn_w_out[0])[:, :, FW * c:FW * (c + 1)])
            chunk(C_FFN, kp(ffn_w1[0])[:, :, 0:FW])
            for h in range(DT):
                if h == 0:
                    sp.wait_ge(sem("q2_ready"), 1)
                if h >= 2:
                    sp.wait_ge(sem("state_out"), 16 * (h - 1))
                sp.dma_start(st[:, h % 2, :, :], state_hgrn[:, 0, h].rearrange("b k v -> k b v")
                             ).then_inc(sem(f"state_in{h % 2}"), 16)
                if h >= 1:
                    out_state(sp, h - 1)
            out_state(sp, DT - 1)

            chunk(C_FFN + 1, kp(ffn_w3[0])[:, :, 0:FW])
            with sp.Fori(0, FB - 1) as i:
                n = i * 3 + (C_FFN + 2)
                chunk(n, kp(ffn_w1[0])[:, :, bass.ds(i * FW + FW, FW)], (C_FFN + 2) % RAW)
                chunk(n + 1, kp(ffn_w3[0])[:, :, bass.ds(i * FW + FW, FW)], (C_FFN + 3) % RAW)
                chunk(n + 2, kp(ffn_w2[0])[:, bass.ds(i * 4, 4), :], (C_FFN + 4) % RAW)
            chunk(C_FFN + 3 * FB - 1, kp(ffn_w2[0])[:, 4 * (FB - 1):4 * FB, :])
            for c in range(6):
                chunk(C_CIN + c, kp(conv_w_in[0])[:, :, FW * c:FW * (c + 1)])
            for c in range(2):
                chunk(C_COUT + c, kp(conv_w_out[0])[:, :, FW * c:FW * (c + 1)])

            def expert(w, e, k0, kn):
                tiles = w.shape[2] // P
                return w[0].rearrange("e (k p) n -> p (e k) n", p=P)[:, bass.ds(e * tiles + k0, kn), :]

            def head(k, e, col):
                pass

            def body(k, e, col, ahead):
                n = k * JOB + C_MOE
                chunk(n, expert(moe_w1, e, 0, DT)[:, :, 0:FW], 0)
                chunk(n + 1, expert(moe_w3, e, 0, DT)[:, :, 0:FW], 1)
                with sp.Fori(0, FB - 1) as i:
                    m = n + i * 3 + 2
                    cols = bass.ds(i * FW + FW, FW)
                    chunk(m, expert(moe_w1, e, 0, DT)[:, :, cols], 2)
                    chunk(m + 1, expert(moe_w3, e, 0, DT)[:, :, cols], 0)
                    chunk(m + 2, expert(moe_w2, e, i * 4, 4), 1)
                chunk(n + (JOB - 1), expert(moe_w2, e, 4 * (FB - 1), 4), 2)
                if not isinstance(k, int):
                    return
                sp.wait_ge(sem("flags"), 1)

            jobs(sp, head, body)

            sp.wait_ge(sem("y_rows"), 2)
            sp.dma_start(y_prompt[0].rearrange("(b p) d -> p b d", p=P), yrows[:, 0:BLK, :]
                         ).then_inc(sem("stored"), 16)
            sp.dma_start(y_sample[:, 0, :], yrows[0:B, BLK, :]).then_inc(sem("stored"), 16)
            sp.wait_ge(sem("stored"), 32)
            sp.wait_ge(sem("state_out"), 16 * DT)
            sp.wait_ge(sem("prompt_state_out"), 32)
            sp.wait_ge(sem("conv_out"), 48)

        @block.gpsimd
        def _(pool):
            g = nc.gpsimd
            made = sem("pool_made")
            g.memset(ident[:, :], 0.0).then_inc(made, 1)
            g.memset(ones[:, :], 1.0).then_inc(made, 1)
            g.memset(causal[:, :], 1.0).then_inc(made, 1)
            g.memset(before[:, :], 1.0).then_inc(made, 1)
            g.memset(eps[:, :], EPS).then_inc(made, 1)
            g.iota(iota[:, :], [[1, P]], base=0, channel_multiplier=0,
                   allow_small_or_imprecise_dtypes=True).then_inc(made, 1)
            pool.wait_ge(made, 6)
            g.affine_select(out=ident[:, :], in_=ident[:, :], compare_op=ALU.not_equal, fill=1.0,
                            base=0, pattern=[[-1, P]], channel_multiplier=1).then_inc(made, 1)
            c3 = causal[:, :].rearrange("p (c t) -> p c t", t=CH)
            g.affine_select(out=causal[:, :], in_=causal[:, :], compare_op=ALU.is_ge, fill=0.0,
                            base=0, pattern=[[1, P]], channel_multiplier=-1).then_inc(made, 1)
            g.affine_select(out=before[:, :], in_=before[:, :], compare_op=ALU.is_gt, fill=0.0,
                            base=0, pattern=[[1, P]], channel_multiplier=-1).then_inc(made, 1)
            pool.wait_ge(made, 9)
            g.affine_select(out=c3, in_=c3, compare_op=ALU.is_ge, fill=0.0,
                            base=0, pattern=[[-CH, CPB], [0, CH]], channel_multiplier=1
                            ).then_inc(sem("consts"), 1)
            for h in range(DT):
                if h == 0:
                    pool.wait_ge(sem("kv_rows"), 1)
                    pool.wait_ge(sem("kv_rows2"), 1)
                if h >= 2:
                    pool.wait_ge(sem("outer_mm"), h - 1)
                g.tensor_tensor(vbd[:, h % 2, :, :],
                                vs[:, h, :].unsqueeze(1).to_broadcast([B, B, P]),
                                ident[0:B, 0:B].unsqueeze(2).to_broadcast([B, B, P]),
                                ALU.mult).then_inc(sem("vbd_ready"), 1)

        @block.scalar
        def _(act):
            a = nc.scalar
            emitted = [0]

            def hi(p, slot, half, buf):
                n3 = (p // 2) // RAW + 1 if isinstance(p, int) else None
                if n3 is not None:
                    act.wait_ge(raw_loaded[slot], 16 * n3)
                    if p >= SPLIT:
                        act.wait_ge(used, p - SPLIT + 1)
                a.activation(whi[:, buf, :], raw[:, slot, PW * half:PW * (half + 1)],
                             ACT.Copy).then_inc(hi_done, 1)

            def split_to(p):
                while emitted[0] < p:
                    q = emitted[0]
                    hi(q, (q // 2) % RAW, q % 2, q % SPLIT)
                    emitted[0] += 1

            def step(p):
                split_to(p + 1 + AHEAD)
                act.wait_ge(used, p + 1)

            def norm(which, split):
                act.wait_ge(sem("x_ready_" + which), 1)
                for j in range(2):
                    a.activation(sq[:, 4 * j:4 * j + 4, :], xT[:, 4 * j:4 * j + 4, :], ACT.Square
                                 ).then_inc(sem("sq_" + which), 1)
                act.wait_ge(sem("ss_done_" + which), 1)
                a.activation(rs[:, :], ss_bank(which)[:, 0:T], ACT.Sqrt, bias=eps[:, :],
                             scale=1.0 / D).then_inc(sem("rs_" + which), 1)
                if split:
                    for j in range(2):
                        act.wait_ge(sem("xn_" + which), 4 * j + 4)
                        a.activation(xh[:, 4 * j:4 * j + 4, :], xn[:, 4 * j:4 * j + 4, :], ACT.Copy
                                     ).then_inc(sem("xh_" + which), 1)

            act.wait_ge(sem("x_turned"), 1)
            a.activation(xT[:, 0:4, :], quad("x0")[:, :, 0:T], ACT.Copy).then_inc(sem("x_ready_half"), 1)
            act.wait_ge(sem("x_ready_half"), 1)
            act.sem_inc(let_go("x0"), 2)
            act.wait_ge(sem("vec_turned"), 1)
            a.activation(vecs[:, :], quad("vec")[:, 0, 0:NV], ACT.Copy).then_inc(sem("vecs_copied"), 1)
            a.activation(bufT[:, :, :, :].rearrange("p d b r -> p (d b r)"),
                         quad("vec")[:, 1, 0:2 * B * DT], ACT.Copy).then_inc(sem("vecs_copied"), 1)
            act.wait_ge(sem("vecs_copied"), 2)
            act.sem_inc(let_go("vec"), 2)
            split_to(1)
            norm("mix0", True)
            act.wait_ge(sem("lb_shifted"), 1)
            a.activation(lbs[:, 0:3, :], lbs[:, 0:3, :], ACT.Exp).then_inc(sem("lb_exp"), 1)

            for c in range(8):
                p = 2 * (C_IN + c)
                kind = c // 2
                step(p)
                step(p + 1)
                fn = (ACT.Silu, ACT.Sigmoid, ACT.Copy, ACT.Silu)[kind]
                a.activation(z[:, 4 * c:4 * c + 4, :], quad(f"in{c}")[:, :, 0:T], fn
                             ).then_inc(sem("z_ready"), 1)
                act.wait_ge(sem("z_ready"), c + 1)
                act.sem_inc(let_go(f"in{c}"), 2)

            for g in range(2):
                act.wait_ge(sem(f"turned{g}"), 1)
                if g:
                    act.wait_ge(sem("o_mm"), g)
                a.activation(vtok[:, :, :, :].rearrange("p b h v -> p b (h v)"),
                             quad(f"t{g}")[:, 0:2, :], ACT.Copy).then_inc(sem("vtok_ready"), 1)
                act.wait_ge(sem("vtok_ready"), g + 1)
                act.sem_inc(let_go(f"t{g}"), 1)
                act.wait_ge(sem("o_mm"), g + 1)
                for b in range(BLK):
                    a.activation(oT[:, 4 * g:4 * g + 4, P * b:P * (b + 1)],
                                 quad(f"o{g}")[:, b, :].rearrange("p (h t) -> p h t", h=4), ACT.Copy
                                 ).then_inc(sem("o_copied"), 1)
                act.wait_ge(sem("o_copied"), 2 * g + 2)
                act.sem_inc(let_go(f"o{g}"), 2)
                act.wait_ge(sem("final_state"), g + 1)
                act.dma_start(hgrn_prompt[0, 0, 4 * g:4 * g + 4].rearrange("h k v -> k h v"),
                              U[:, NC - 1, :, :]).then_inc(sem("prompt_state_out"), 16)
            act.wait_ge(sem("ts_turned"), 1)
            act.wait_ge(sem("prompt_state_out"), 32)
            a.activation(vs[:, :, :].rearrange("b h v -> b (h v)").rearrange("b (j n) -> b j n", j=2),
                         quad("ts")[0:B, 0:2, :], ACT.Copy).then_inc(sem("kv_rows"), 1)
            act.wait_ge(sem("kv_rows"), 1)
            act.sem_inc(let_go("ts"), 1)
            act.wait_ge(sem("state_read"), DT)
            a.activation(oT[:, :, TP:T], quad("os")[:, 0, 0:DT * B].rearrange("p (h b) -> p h b", h=DT),
                         ACT.Copy).then_inc(sem("os_copied"), 1)
            act.wait_ge(sem("os_copied"), 1)
            act.sem_inc(let_go("os"), 2)
            osq = pb
            for j in range(2):
                a.activation(osq[:, 4 * j:4 * j + 4, :], oT[:, 4 * j:4 * j + 4, :], ACT.Square
                             ).then_inc(sem("osq"), 1)
            for j in range(2):
                act.wait_ge(sem(f"on_mm{j}"), 1)
                a.activation(rs4[:, j, :, :], quad(f"on{j}")[:, :, 0:T], ACT.Sqrt, bias=eps[:, :],
                             scale=1.0 / P).then_inc(sem("rs4"), 1)
                act.wait_ge(sem("rs4"), j + 1)
                act.sem_inc(let_go(f"on{j}"), 2)
            for j in range(2):
                act.wait_ge(sem("gated"), 4 * j + 4)
                a.activation(xh[:, 4 * j:4 * j + 4, :], z[:, 4 * j:4 * j + 4, :], ACT.Copy
                             ).then_inc(sem("xh_out"), 1)
            split_to(2 * C_FFN + AHEAD)
            norm("ffn0", True)

            P0 = 2 * C_FFN

            def ffn_silu(b, p):
                act.wait_ge(used, p)
                if not isinstance(b, int) or b >= 1:
                    act.wait_ge(sem("fx_ready"), b)
                a.activation(fs[:, :, :], Q[0][:, :, 0:T], ACT.Silu).then_inc(sem("fs_ready"), 1)

            def ffn_high(b, w2_used):
                act.wait_ge(sem("fx_ready"), b + 1)
                if w2_used is not None:
                    act.wait_ge(used, w2_used)
                a.activation(fh[:, :, :], fx[:, :, :], ACT.Copy).then_inc(sem("fh_ready"), 1)

            def hi_rel(base, reg):
                n = base // 2
                act.wait_ge(raw_loaded[n % RAW], (reg + (n // RAW + 1)) * 16)
                act.wait_ge(used, reg * 6 + (base - SPLIT + 1))
                a.activation(whi[:, base % SPLIT, :],
                             raw[:, n % RAW, PW * (base % 2):PW * (base % 2 + 1)],
                             ACT.Copy).then_inc(hi_done, 1)

            split_to(P0 + 4)
            ffn_silu(0, P0 + 2)
            split_to(P0 + 6)
            ffn_high(0, None)
            with act.Fori(0, FB - 1) as i:
                b0 = P0 + 4
                hi_rel(b0 + 2, i)
                hi_rel(b0 + 3, i)
                ffn_silu(i + 1, i * 6 + (b0 + 2))
                hi_rel(b0 + 4, i)
                hi_rel(b0 + 5, i)
                hi_rel(b0 + 6, i)
                hi_rel(b0 + 7, i)
                ffn_high(i + 1, i * 6 + (b0 + 6))
            emitted[0] = P0 + 4 + 6 * (FB - 1) + 2
            split_to(2 * C_CIN)
            norm("mix1", True)
            split_to(2 * C_CIN + AHEAD)
            for c in range(6):
                p = 2 * (C_CIN + c)
                step(p)
                step(p + 1)
                if c < 4:
                    a.activation(zc[:, 4 * c:4 * c + 4, :], quad(f"cin{c}")[:, :, 0:T], ACT.Copy
                                 ).then_inc(sem("zc_ready"), 1)
                    act.wait_ge(sem("zc_ready"), c + 1)
                    act.sem_inc(let_go(f"cin{c}"), 2)
            act.wait_ge(sem("cg_turned"), 1)
            a.activation(cgr[:, :].rearrange("r (j n) -> r j n", j=2), quad("cg")[0:2 + B, 0:2, :],
                         ACT.Copy).then_inc(sem("cg_rows"), 1)
            act.wait_ge(sem("cg_rows"), 1)
            act.sem_inc(let_go("cg"), 2)
            act.dma_start(conv_prompt[0, 0], cgr[0:2, :]).then_inc(sem("conv_out"), 16)
            act.dma_start(conv_sample[:, 0, 1, :], cgr[2:2 + B, :]).then_inc(sem("conv_out"), 16)
            act.dma_start(conv_sample[:, 0, 0, :], state_conv[:, 0, 1, :]).then_inc(sem("conv_out"), 16)
            for j in range(2):
                act.wait_ge(sem("by"), 2 * j + 2)
                a.activation(xh[:, 4 * j:4 * j + 4, :], xn[:, 4 * j:4 * j + 4, :], ACT.Copy
                             ).then_inc(sem("xh_cout"), 1)
            split_to(2 * C_MOE)
            norm("ffn1", False)
            act.wait_ge(sem("conv_out"), 48)
            act.wait_ge(sem("top_gap"), 1)
            a.activation(tk[:, 4, :], tk[:, 3, :], ACT.Exp).then_inc(sem("top_exp"), 1)
            act.wait_ge(sem("xt_turned"), 1)
            a.activation(xtok[:, 0, :].rearrange("p (j n) -> p j n", j=2), quad("xt0")[:, 0:2, :],
                         ACT.Copy).then_inc(sem("xtok_act"), 1)
            act.wait_ge(sem("xtok_act"), 1)
            act.sem_inc(let_go("xt0"), 2)
            act.wait_ge(sem("xt_turned"), 3)
            a.activation(xtok[0:B, 2, :].rearrange("p (j n) -> p j n", j=2), quad("xt2")[0:B, 0:2, :],
                         ACT.Copy).then_inc(sem("xtok_act"), 1)

            M0 = 2 * C_MOE
            act.wait_ge(sem("moe_ready"), 1)

            def hi_m(k, q0, q1, reg=None):
                for q in range(q0, q1):
                    n = q // 2
                    loads = k * (JOB // RAW) + (n // RAW + C_MOE // RAW + 1)
                    free = k * (2 * JOB) + (M0 + q - SPLIT_M + 1)
                    if reg is not None:
                        loads, free = loads + reg, free + reg * 6
                    act.wait_ge(raw_loaded[n % RAW], loads * 16)
                    act.wait_ge(used, free)
                    a.activation(bufs(q)[0], raw[:, n % RAW, PW * (q % 2):PW * (q % 2 + 1)],
                                 ACT.Copy).then_inc(hi_done, 1)

            def silu(nth, last):
                act.wait_ge(used, last)
                act.wait_ge(sem("hx_ready"), nth + 1)
                a.activation(hs[:, :], Q[0][:, 0, :], ACT.Silu).then_inc(sem("hs_ready"), 1)

            def gathered(k):
                act.wait_ge(sem("xg_mm"), k + 1)
                act.wait_ge(used, k * (2 * JOB) + (M0 - 2))
                a.activation(xgh[:, :, :].rearrange("p (j d) s -> p j (d s)", j=2), Q[1][:, 2:4, :],
                             ACT.Copy).then_inc(sem("xgh_ready"), 1)

            def head(k, e, col):
                hi_m(k, 0, AHEAD_M)
                gathered(k)
                hi_m(k, AHEAD_M, AHEAD_M + 2)
                silu(k * FB, k * (2 * JOB) + (M0 + 2))

            def body(k, e, col, ahead):
                pk = k * (2 * JOB) + M0

                def high(nth, w2_used):
                    act.wait_ge(sem("h_turned"), nth + 1)
                    act.wait_ge(used, w2_used)
                    a.activation(hth[:, :, :].rearrange("p a s -> p (a s)"), Q[0][:, 2, :], ACT.Copy
                                 ).then_inc(sem("hth_ready"), 1)

                def block(i, q, reg):
                    hi_m(k, q, q + 2, reg)
                    silu(kb + i + 1, pk + i * 6 + 6)
                    high(kb + i, pk + i * 6 + 4)
                    hi_m(k, q + 2, q + 6 if reg is not None or ahead else 2 * JOB, reg)

                kb = k * FB
                hi_m(k, AHEAD_M + 2, AHEAD_M + 3)
                act.wait_ge(sem("pwt_mm"), k + 1)
                act.wait_ge(sem("scatter_mm"), k * DT + DT)
                a.activation(pwt[:, :], Q[0][:, 3, 0:T], ACT.Copy).then_inc(sem("pwt_ready"), 1)
                hi_m(k, AHEAD_M + 3, AHEAD_M + 4)
                with act.Fori(0, FB - 2) as i:
                    block(i, AHEAD_M + 4, i)
                block(FB - 2, AHEAD_M + 4 + 6 * (FB - 2), None)
                high(kb + (FB - 1), pk + (6 * (FB - 1) + 4))
                if ahead:
                    hi_m(k, 2 * JOB + AHEAD_M - 2, 2 * JOB + AHEAD_M - 1)
                    gathered(k + 1)
                    hi_m(k, 2 * JOB + AHEAD_M - 1, 2 * JOB + AHEAD_M)
                act.wait_ge(used, pk + 2 * JOB)
                a.activation(ysb[:, 0:512], Q[1][:, 0, :], ACT.Copy).then_inc(sem("y_act"), 1)
                if ahead:
                    hi_m(k, 2 * JOB + AHEAD_M, 2 * JOB + AHEAD_M + 2)
                    silu((k + 1) * FB, pk + (2 * JOB + 2))

            jobs(act, head, body)
            norm("final", False)
            act.wait_ge(sem("y_turned"), 1)
            a.activation(yrows[:, 0, :].rearrange("p (j n) -> p j n", j=2), Q[1][:, 0:2, :],
                         ACT.Copy).then_inc(sem("y_row0"), 1)
            act.wait_ge(sem("y_turned"), 3)
            a.activation(yrows[0:B, 2, :].rearrange("p (j n) -> p j n", j=2), Q[0][0:B, 0:2, :],
                         ACT.Copy).then_inc(sem("y_rows"), 1)
            act.wait_ge(sem("y_row0"), 1)

        @block.vector
        def _(dve):
            v = nc.vector
            emitted = [0]
            chained = [0]

            def then(ins):
                chained[0] += 1
                ins.then_inc(sem("dve_chain"), 1)
                dve.wait_ge(sem("dve_chain"), chained[0])

            def lo_ins(slot, half, high, low):
                v.tensor_tensor(low, raw[:, slot, PW * half:PW * (half + 1)],
                                high.bitcast(F32), ALU.subtract).then_inc(lo_done, 1)

            def split_to(p):
                while emitted[0] < p:
                    q = emitted[0]
                    dve.wait_ge(hi_done, q + 1)
                    lo_ins((q // 2) % RAW, q % 2, whi[:, q % SPLIT, :], wlo[:, q % SPLIT, :])
                    emitted[0] += 1

            def step(p):
                split_to(p + 1 + AHEAD)
                dve.wait_ge(used, p + 1)

            def vec(name, d):
                return vecs[:, VN[name] + d:VN[name] + d + 1]

            def norm(which, split, gain):
                dve.wait_ge(sem("rs_" + which), 1)
                if which != "final":
                    dve.sem_inc(let_go("ss_" + which), 2)
                then(v.reciprocal(rstd[:, :], rs[:, :]))
                for d in range(DT):
                    v.scalar_tensor_tensor(out=xn[:, d, :], in0=xT[:, d, :], scalar=vec(gain, d),
                                           in1=rstd[:, :], op0=ALU.mult, op1=ALU.mult
                                           ).then_inc(sem("xn_" + which), 1)
                if split:
                    for j in range(2):
                        dve.wait_ge(sem("xh_" + which), j + 1)
                        v.tensor_tensor(xl[:, 4 * j:4 * j + 4, :], xn[:, 4 * j:4 * j + 4, :],
                                        xh[:, 4 * j:4 * j + 4, :].bitcast(F32), ALU.subtract
                                        ).then_inc(sem("xl_" + which), 1)

            dve.wait_ge(sem("x_turned"), 2)
            then(v.tensor_copy(xT[:, 4:8, :], quad("x1")[:, :, 0:T]))
            dve.sem_inc(let_go("x1"), 2)
            dve.wait_ge(sem("x_ready_half"), 1)
            dve.sem_inc(sem("x_ready_mix0"), 1)
            dve.wait_ge(sem("vecs_copied"), 2)
            norm("mix0", True, "mix0")
            split_to(1)
            l = [vecs[:, VN[f"lb{i}"]:VN[f"lb{i}"] + DT] for i in range(3)]
            then(v.tensor_tensor(lbs[:, 3, :], l[0], l[1], ALU.max))
            then(v.tensor_tensor(lbs[:, 3, :], lbs[:, 3, :], l[2], ALU.max))
            for i in range(3):
                ins = v.tensor_tensor(lbs[:, i, :], l[i], lbs[:, 3, :], ALU.subtract)
                then(ins)
            dve.sem_inc(sem("lb_shifted"), 1)
            split_to(2)
            dve.wait_ge(sem("lb_exp"), 1)
            then(v.tensor_tensor(lbs[:, 3, :], lbs[:, 0, :], lbs[:, 1, :], ALU.add))
            then(v.tensor_tensor(lbs[:, 3, :], lbs[:, 3, :], lbs[:, 2, :], ALU.add))
            then(v.reciprocal(lbs[:, 3, :], lbs[:, 3, :]))
            then(v.tensor_tensor(lbs[:, 4, :], lbs[:, 0, :], lbs[:, 3, :], ALU.mult))
            then(v.tensor_scalar(lbs[:, 5, :], lbs[:, 4, :], -1.0, 1.0, ALU.mult, ALU.add))
            zf = z[:, DT:2 * DT, :]
            for c in range(8):
                p = 2 * (C_IN + c)
                step(p)
                step(p + 1)
                if c == 3:
                    dve.wait_ge(sem("z_ready"), 4)
                    for h in range(DT):
                        v.tensor_scalar(zf[:, h, :], zf[:, h, :], lbs[:, 5, h:h + 1],
                                        lbs[:, 4, h:h + 1], ALU.mult, ALU.add
                                        ).then_inc(sem("f_ready"), 1)
                if c == 4:
                    dve.wait_ge(sem("f_ready"), DT)
                    then(v.tensor_scalar(kk[:, :, :], zf, -1.0, 1.0, ALU.mult, ALU.add))
                    v.memset(pb[:, :, :], 0.0).then_inc(sem("pab"), 1)
                    v.tensor_copy(pa[:, :, :], zf).then_inc(sem("pab"), 1)
                    dve.wait_ge(sem("pab"), 2)
                    v.memset(pa[:, :, 0:T:CH], 0.0).then_inc(sem("pab"), 1)
                    v.tensor_copy(pb[:, :, 0:T:CH], zf[:, :, 0:T:CH]).then_inc(sem("pab"), 1)
                    dve.wait_ge(sem("pab"), 4)
                if c == 5:
                    flat = "p h t -> p (h t)"
                    then(v.tensor_tensor_scan(pa[:, :, :].rearrange(flat),
                                              pa[:, :, :].rearrange(flat),
                                              pb[:, :, :].rearrange(flat), 0.0, ALU.mult, ALU.add))
                if c == 6:
                    then(v.tensor_copy(plast[:, :, :], pa[:, :, CH - 1:TP:CH]))
                    then(v.reciprocal(pb[:, :, :], pa[:, :, :]))
            then(v.tensor_tensor(pb[:, :, :], kk[:, :, :], pb[:, :, :], ALU.mult))
            dve.sem_inc(sem("k_in_ready"), 1)
            zq = z[:, 0:DT, :]
            then(v.tensor_tensor(zq[:, :, 0:TP], zq[:, :, 0:TP], pa[:, :, 0:TP], ALU.mult))
            def chunks(t, c0, c1):
                return t[:, :, CH * c0:CH * c1].rearrange("p h (c t) -> p h c t", t=CH)
            then(v.tensor_tensor(
                chunks(zf, 1, NC), chunks(zq, 1, NC),
                plast[:, :, 0:NC - 1].unsqueeze(3).to_broadcast([P, DT, NC - 1, CH]), ALU.mult))
            dve.sem_inc(sem("q2_ready"), 1)
            for g in range(2):
                dve.wait_ge(sem(f"turned{g}"), 1)
                if g:
                    dve.wait_ge(sem("o_mm"), g)
                then(v.tensor_copy(ktok[:, :, :, :].rearrange("p b h k -> p b (h k)"),
                                   quad(f"t{g}")[:, 2:4, :]))
                dve.sem_inc(sem("ktok_ready"), 1)
                dve.sem_inc(let_go(f"t{g}"), 1)
                dve.wait_ge(sem(f"a_mm{g}"), 1)
                then(v.tensor_tensor(
                    amask[:, :, :, :].rearrange("p b h t -> p (b h) t"),
                    quad(f"a{g}")[:, 0:2, :].rearrange("p b (h t) -> p (b h) t", h=4),
                    causal[:, :].unsqueeze(1).to_broadcast([P, BLK * 4, P]), ALU.mult))
                dve.sem_inc(sem("amask_ready"), 1)
                dve.sem_inc(let_go(f"a{g}"), 2)
                if g:
                    dve.wait_ge(sem("prompt_state_out"), 16 * g)
                for c in range(NC):
                    b, j = c // CPB, c % CPB
                    if j == 0:
                        dve.wait_ge(sem("d_mm"), g * BLK + b + 1)
                    d = quad(f"d{g}{b}")
                    for h in range(4):
                        if c == 0:
                            ins = v.tensor_copy(U[:, 0, h, :], d[:, j, P * h:P * (h + 1)])
                        else:
                            ins = v.scalar_tensor_tensor(
                                out=U[:, c, h, :], in0=U[:, c - 1, h, :],
                                scalar=plast[:, 4 * g + h, c - 1:c], in1=d[:, j, P * h:P * (h + 1)],
                                op0=ALU.mult, op1=ALU.add)
                        ins.then_inc(sem("u_ready"), 1)
                    dve.wait_ge(sem("u_ready"), 4 * (g * NC + c + 1))
                    if j == CPB - 1:
                        dve.sem_inc(let_go(f"d{g}{b}"), 2)
                for h in range(4):
                    ins = v.tensor_scalar(U[:, NC - 1, h, :], U[:, NC - 1, h, :],
                                          plast[:, 4 * g + h, NC - 1:NC], None, ALU.mult)
                    then(ins)
                dve.sem_inc(sem("final_state"), 1)
            dve.wait_ge(sem("ts_turned"), 1)
            dve.wait_ge(sem("prompt_state_out"), 32)
            then(v.tensor_copy(ks[:, :, :].rearrange("b h v -> b (h v)").rearrange("b (j n) -> b j n", j=2),
                               quad("ts")[0:B, 2:4, :]))
            dve.sem_inc(sem("kv_rows2"), 1)
            dve.sem_inc(let_go("ts"), 1)
            for h in range(DT):
                dve.wait_ge(sem("outer_mm"), h + 1)
                dve.wait_ge(sem(f"state_in{h % 2}"), 16 * (h // 2 + 1))
                o = quad("outer")[:, 2 * (h % 2):2 * (h % 2) + 2, :].rearrange(
                    "p j (b v) -> p (j b) v", b=4)
                for b in range(B):
                    ins = v.scalar_tensor_tensor(
                        out=st[:, h % 2, b, :], in0=st[:, h % 2, b, :],
                        scalar=zf[:, h, TP + b:TP + b + 1], in1=o[:, b, :],
                        op0=ALU.mult, op1=ALU.add)
                    ins.then_inc(sem("state_b"), 1)
                dve.wait_ge(sem("state_b"), B * (h + 1))
                dve.sem_inc(sem("state_new"), 1)
            dve.sem_inc(let_go("outer"), 2)
            zg = z[:, 3 * DT:4 * DT, :]
            for j in range(2):
                dve.wait_ge(sem("rs4"), j + 1)
                then(v.reciprocal(rs4[:, j, :, :], rs4[:, j, :, :]))
                then(v.tensor_tensor(oT[:, 4 * j:4 * j + 4, :], oT[:, 4 * j:4 * j + 4, :],
                                     rs4[:, j, :, :], ALU.mult))
                for h in range(4 * j, 4 * j + 4):
                    v.scalar_tensor_tensor(out=z[:, h, :], in0=oT[:, h, :], scalar=vec("gn", h),
                                           in1=zg[:, h, :], op0=ALU.mult, op1=ALU.mult
                                           ).then_inc(sem("gated"), 1)
            for j in range(2):
                dve.wait_ge(sem("xh_out"), j + 1)
                v.tensor_tensor(xl[:, 4 * j:4 * j + 4, :], z[:, 4 * j:4 * j + 4, :],
                                xh[:, 4 * j:4 * j + 4, :].bitcast(F32), ALU.subtract
                                ).then_inc(sem("xl_out"), 1)

            def add_quad(name, c, p):
                step(p)
                step(p + 1)
                then(v.tensor_tensor(xT[:, 4 * c:4 * c + 4, :], xT[:, 4 * c:4 * c + 4, :],
                                     quad(name)[:, :, 0:T], ALU.add))
                dve.sem_inc(let_go(name), 2)

            for c in range(2):
                add_quad(f"out{c}", c, 2 * (C_OUT + c) if c == 0 else 2 * (C_OUT + c) - 0)
            dve.sem_inc(sem("x_ready_ffn0"), 1)
            norm("ffn0", True, "ffn0")

            P0 = 2 * C_FFN
            split_to(P0 + 4)

            def lo_rel(base, reg):
                n = base // 2
                dve.wait_ge(hi_done, reg * 6 + (base + 1))
                lo_ins(n % RAW, base % 2, whi[:, base % SPLIT, :], wlo[:, base % SPLIT, :])

            def ffn_mul(b, last):
                dve.wait_ge(used, last)
                dve.wait_ge(sem("fs_ready"), b + 1)
                if not isinstance(b, int) or b >= 1:
                    dve.wait_ge(sem("fl_ready"), b)
                v.tensor_tensor(fx[:, :, :], fs[:, :, :], Q[1][:, :, 0:T], ALU.mult
                                ).then_inc(sem("fx_ready"), 1)

            def ffn_low(b):
                dve.wait_ge(sem("fh_ready"), b + 1)
                v.tensor_tensor(fl[:, :, :], fx[:, :, :], fh[:, :, :].bitcast(F32), ALU.subtract
                                ).then_inc(sem("fl_ready"), 1)

            def ffn_add(b, j, last):
                if j == 0:
                    dve.wait_ge(sem("w2_half"), b + 1)
                else:
                    dve.wait_ge(used, last)
                v.tensor_tensor(xT[:, 4 * j:4 * j + 4, :], xT[:, 4 * j:4 * j + 4, :],
                                Q[j][:, :, 0:T], ALU.add).then_inc(sem("x_added"), 1)

            dve.sem_inc(sem("x_added"), 2)
            split_to(P0 + 6)
            ffn_mul(0, P0 + 4)
            ffn_low(0)
            with dve.Fori(0, FB - 1) as i:
                b0 = P0 + 4
                lo_rel(b0 + 2, i)
                lo_rel(b0 + 3, i)
                lo_rel(b0 + 4, i)
                lo_rel(b0 + 5, i)
                ffn_mul(i + 1, i * 6 + (b0 + 4))
                lo_rel(b0 + 6, i)
                ffn_add(i, 0, None)
                lo_rel(b0 + 7, i)
                ffn_add(i, 1, i * 6 + (b0 + 6))
                ffn_low(i + 1)
            emitted[0] = P0 + 4 + 6 * (FB - 1) + 2
            ffn_add(FB - 1, 0, None)
            ffn_add(FB - 1, 1, P0 + 4 + 6 * (FB - 1) + 2)
            dve.wait_ge(sem("x_added"), 2 + 2 * FB)
            dve.sem_inc(sem("x_ready_mix1"), 1)
            norm("mix1", True, "mix1")

            S0 = 2 + TP
            ues = ue[:, :, S0:UE].rearrange("p d (b r) -> p d b r", r=3)
            v.memset(ue[:, :, 0:2], 0.0).then_inc(sem("ue_ready"), 1)
            v.tensor_copy(ues[:, :, :, 0:2], bufT[:, :, :, :]).then_inc(sem("ue_ready"), 1)
            zb, zcc = zc[:, 0:DT, :], zc[:, DT:2 * DT, :]
            for c in range(6):
                p = 2 * (C_CIN + c)
                step(p)
                step(p + 1)
                if c >= 4:
                    j = c - 4
                    ds = slice(4 * j, 4 * j + 4)
                    dve.wait_ge(sem("zc_ready"), 4)
                    v.tensor_tensor(ue[:, ds, 2:S0], zcc[:, ds, 0:TP], quad(f"cin{c}")[:, :, 0:TP],
                                    ALU.mult).then_inc(sem("ue_ready"), 1)
                    v.tensor_tensor(ues[:, ds, :, 2], zcc[:, ds, TP:T], quad(f"cin{c}")[:, :, TP:T],
                                    ALU.mult).then_inc(sem("ue_ready"), 1)
                    dve.wait_ge(sem("ue_ready"), 2 * j + 4)
                    dve.sem_inc(let_go(f"cin{c}"), 2)
                    for d in range(4 * j, 4 * j + 4):
                        n = UE - 2
                        v.tensor_scalar(yc[:, d, :], ue[:, d, 0:n], vec("cw0", d), None, ALU.mult
                                        ).then_inc(sem("yc0"), 1)
                    for tap in (1, 2):
                        for d in range(4 * j, 4 * j + 4):
                            dve.wait_ge(sem(f"yc{tap - 1}"), d + 1)
                            v.scalar_tensor_tensor(out=yc[:, d, :], in0=ue[:, d, tap:tap + n],
                                                   scalar=vec(f"cw{tap}", d), in1=yc[:, d, :],
                                                   op0=ALU.mult, op1=ALU.add
                                                   ).then_inc(sem(f"yc{tap}"), 1)
                    dve.wait_ge(sem("yc2"), 4 * j + 4)
                    v.tensor_tensor(xn[:, ds, 0:TP], zb[:, ds, 0:TP], yc[:, ds, 0:TP], ALU.mult
                                    ).then_inc(sem("by"), 1)
                    v.tensor_tensor(xn[:, ds, TP:T], zb[:, ds, TP:T], yc[:, ds, S0:UE - 2:3],
                                    ALU.mult).then_inc(sem("by"), 1)
            v.tensor_copy(cg[:, :, 0:2], ue[:, :, TP:S0]).then_inc(sem("cg_ready"), 1)
            v.tensor_copy(cg[:, :, 2:2 + B], ues[:, :, :, 2]).then_inc(sem("cg_ready"), 1)
            for j in range(2):
                dve.wait_ge(sem("xh_cout"), j + 1)
                v.tensor_tensor(xl[:, 4 * j:4 * j + 4, :], xn[:, 4 * j:4 * j + 4, :],
                                xh[:, 4 * j:4 * j + 4, :].bitcast(F32), ALU.subtract
                                ).then_inc(sem("xl_cout"), 1)
            for c in range(2):
                if c == 0:
                    step(2 * C_COUT)
                    step(2 * C_COUT + 1)
                else:
                    split_to(2 * C_MOE)
                    dve.wait_ge(used, 2 * C_COUT + 4)
                then(v.tensor_tensor(xT[:, 4 * c:4 * c + 4, :], xT[:, 4 * c:4 * c + 4, :],
                                     quad(f"cout{c}")[:, :, 0:T], ALU.add))
                dve.sem_inc(let_go(f"cout{c}"), 2)
            dve.sem_inc(sem("x_ready_ffn1"), 1)
            norm("ffn1", False, "ffn1")

            dve.wait_ge(sem("conv_out"), 48)
            then(v.memset(lg[:, :, :], 0.0))
            dve.wait_ge(sem("lg_mm"), 1)
            then(v.tensor_copy(lg[:, 0:BLK, :], quad("lg")[:, 0, 0:BLK * E].rearrange(
                "p (t e) -> p t e", e=E)))
            then(v.tensor_copy(lg[0:B, BLK, :], quad("lg")[0:B, 0, BLK * E:TT * E]))
            dve.sem_inc(let_go("lg"), 2)
            then(v.tensor_scalar(iote[:, :], iota[:, 0:E], -1.0, float(E), ALU.mult, ALU.add))
            then(v.memset(valid[:, :], 1.0))
            then(v.reduce_sum(tk[:, 9, 0:1], before[:, :], AX.X))
            then(v.tensor_scalar(valid[:, BLK:TT], tk[:, 9, 0:1], float(P - 1 - B), None, ALU.is_gt))

            def bc(t):
                return t.unsqueeze(2).to_broadcast([P, TT, E])

            iob = iote[:, :].unsqueeze(1).to_broadcast([P, TT, E])
            for n, oh in ((0, oh1), (1, oh2)):
                then(v.tensor_reduce(tk[:, n, :], lg[:, :, :], AX.X, ALU.max))
                then(v.tensor_tensor(wt[:, :, :], lg[:, :, :], bc(tk[:, n, :]), ALU.is_equal))
                then(v.tensor_tensor(wt[:, :, :], wt[:, :, :], iob, ALU.mult))
                then(v.tensor_reduce(tk[:, 2, :], wt[:, :, :], AX.X, ALU.max))
                then(v.tensor_tensor(oh[:, :, :], wt[:, :, :], bc(tk[:, 2, :]), ALU.is_equal))
                if n == 0:
                    then(v.scalar_tensor_tensor(out=lg[:, :, :], in0=oh[:, :, :], scalar=-3e38,
                                                in1=lg[:, :, :], op0=ALU.mult, op1=ALU.add))
            then(v.tensor_tensor(tk[:, 3, :], tk[:, 1, :], tk[:, 0, :], ALU.subtract))
            dve.sem_inc(sem("top_gap"), 1)
            for oh in (oh1, oh2):
                then(v.tensor_tensor(oh[:, :, :], oh[:, :, :], bc(valid[:, :]), ALU.mult))
            then(v.tensor_tensor(sel[:, :, :], oh1[:, :, :], oh2[:, :, :], ALU.add))
            dve.sem_inc(sem("sel_ready"), 1)
            dve.wait_ge(sem("top_exp"), 1)
            then(v.tensor_scalar(tk[:, 5, :], tk[:, 4, :], 1.0, None, ALU.add))
            then(v.reciprocal(tk[:, 6, :], tk[:, 5, :]))
            then(v.tensor_tensor(tk[:, 7, :], tk[:, 4, :], tk[:, 6, :], ALU.mult))
            then(v.tensor_tensor(wt[:, :, :], oh1[:, :, :], bc(tk[:, 6, :]), ALU.mult))
            then(v.tensor_tensor(oh2[:, :, :], oh2[:, :, :], bc(tk[:, 7, :]), ALU.mult))
            then(v.tensor_tensor(wt[:, :, :], wt[:, :, :], oh2[:, :, :], ALU.add))
            dve.wait_ge(sem("rank_mm"), 1)
            rk = quad("rank")[:, 0, 0:TT * E].rearrange("p (t e) -> p t e", e=E)
            then(v.scalar_tensor_tensor(out=ptab[:, :, 0:E], in0=rk, scalar=1.0, in1=sel[:, :, :],
                                        op0=ALU.add, op1=ALU.mult))
            then(v.tensor_copy(cnt[:, :], quad("rank")[:, 0, TT * E:(TT + 1) * E]))
            dve.sem_inc(let_go("rank"), 2)
            then(v.tensor_scalar(ptab[:, :, 0:E], ptab[:, :, 0:E], -1.0, None, ALU.add))
            for c in (1, 2):
                then(v.tensor_scalar(ptab[:, :, c * E:(c + 1) * E], ptab[:, :, 0:E],
                                     float(-P * c), None, ALU.add))
                then(v.tensor_scalar(flag[:, c * E:(c + 1) * E], cnt[:, :], float(P * c), None,
                                     ALU.is_gt))
            then(v.tensor_reduce(tk[:, 8, 0:1], cnt[:, :], AX.X, ALU.max))
            then(v.tensor_scalar(flag[:, NS:NS + 1], tk[:, 8, 0:1], float(P), None, ALU.is_gt))
            then(v.memset(zero[:, :], 0.0))
            dve.wait_ge(sem("xt_turned"), 2)
            then(v.tensor_copy(xtok[:, 1, :].rearrange("p (j n) -> p j n", j=2),
                               quad("xt1")[:, 0:2, :]))
            dve.sem_inc(let_go("xt1"), 2)
            dve.wait_ge(sem("xtok_act"), 2)
            dve.sem_inc(sem("hx_ready"), 1)
            dve.sem_inc(sem("y_dve"), 1)
            dve.sem_inc(sem("x_scattered"), DT)
            dve.sem_inc(sem("scatter_mm"), DT)
            dve.sem_inc(sem("flags"), 1)
            dve.sem_inc(sem("moe_ready"), 1)

            M0 = 2 * C_MOE

            def lo_m(k, q0, q1, reg=None):
                for q in range(q0, q1):
                    w = k * (2 * JOB) + (M0 + q + 1)
                    dve.wait_ge(hi_done, w if reg is None else w + reg * 6)
                    lo_ins((q // 2) % RAW, q % 2, *bufs(q))

            def places(k, e, col):
                for t in range(TT):
                    r = rows[t]
                    v.tensor_scalar(pm[0:r, t, :], iota[0:r, :], ptab[0:r, t, bass.ds(col, 1)],
                                    None, ALU.is_equal).then_inc(sem("pm_ready"), 1)
                for t in range(TT):
                    r = rows[t]
                    v.tensor_scalar(pw[0:r, t, :], iota[0:r, :], ptab[0:r, t, bass.ds(col, 1)],
                                    wt[0:r, t, bass.ds(e, 1)], ALU.is_equal, ALU.mult
                                    ).then_inc(sem("pm_ready"), 1)

            def gathered(k):
                dve.wait_ge(sem("xgh_ready"), k + 1)
                v.tensor_tensor(xgl[:, :, :].rearrange("p (j d) s -> p j (d s)", j=2),
                                Q[1][:, 2:4, :],
                                xgh[:, :, :].rearrange("p (j d) s -> p j (d s)", j=2).bitcast(F32),
                                ALU.subtract).then_inc(sem("xgl_ready"), 1)

            def scattered(k):
                for d in range(DT):
                    dve.wait_ge(sem("scatter_mm"), k * DT + (DT + d + 1))
                    v.tensor_tensor(xT[:, d, :], xT[:, d, :], Q[1][:, 2 + d % 2, 0:T], ALU.add
                                    ).then_inc(sem("x_scattered"), 1)

            def head(k, e, col):
                places(k, e, col)
                lo_m(k, 0, AHEAD_M)
                gathered(k)
                lo_m(k, AHEAD_M, AHEAD_M + 2)

            def body(k, e, col, ahead):
                pk = k * (2 * JOB) + M0

                def mul(nth, last):
                    dve.wait_ge(used, last)
                    dve.wait_ge(sem("hs_ready"), nth + 1)
                    v.tensor_tensor(hx[:, :], hs[:, :], Q[0][:, 1, :], ALU.mult
                                    ).then_inc(sem("hx_ready"), 1)

                def low(nth):
                    dve.wait_ge(sem("hth_ready"), nth + 1)
                    v.tensor_tensor(htl[:, :, :].rearrange("p a s -> p (a s)"), Q[0][:, 2, :],
                                    hth[:, :, :].rearrange("p a s -> p (a s)").bitcast(F32),
                                    ALU.subtract).then_inc(sem("htl_ready"), 1)

                def block(i, q, reg):
                    lo_m(k, q, q + 2, reg)
                    low(kb + i)
                    lo_m(k, q + 2, q + 4 if reg is not None or ahead else 2 * JOB, reg)
                    mul(kb + i + 1, pk + i * 6 + 8)
                    if reg is not None or ahead:
                        lo_m(k, q + 4, q + 6, reg)

                kb = k * FB
                lo_m(k, AHEAD_M + 2, AHEAD_M + 4)
                mul(kb, pk + 4)
                if ahead:
                    dve.wait_ge(sem("pwt_mm"), k + 1)
                    places(k + 1, e + 1, col + 1)
                with dve.Fori(0, FB - 2) as i:
                    block(i, AHEAD_M + 4, i)
                block(FB - 2, AHEAD_M + 4 + 6 * (FB - 2), None)
                low(kb + (FB - 1))
                if ahead:
                    lo_m(k, 2 * JOB + AHEAD_M - 2, 2 * JOB + AHEAD_M - 1)
                    gathered(k + 1)
                    lo_m(k, 2 * JOB + AHEAD_M - 1, 2 * JOB + AHEAD_M)
                dve.wait_ge(used, pk + 2 * JOB)
                v.tensor_copy(ysb[:, 512:1024], Q[1][:, 1, :]).then_inc(sem("y_dve"), 1)
                if ahead:
                    lo_m(k, 2 * JOB + AHEAD_M, 2 * JOB + AHEAD_M + 2)
                scattered(k)
                dve.wait_ge(sem("x_scattered"), k * DT + 2 * DT)

            jobs(dve, head, body)
            dve.sem_inc(sem("x_ready_final"), 1)
            norm("final", False, "final")
            dve.wait_ge(sem("y_turned"), 2)
            v.tensor_copy(yrows[:, 1, :].rearrange("p (j n) -> p j n", j=2), Q[1][:, 2:4, :]
                          ).then_inc(sem("y_row1"), 1)
            dve.wait_ge(sem("y_row1"), 1)
            dve.wait_ge(sem("y_row0"), 1)
            dve.sem_inc(sem("y_rows"), 1)

        @block.tensor
        def _(pe):
            t_ = nc.tensor
            pe.wait_ge(sem("consts"), 1)
            pe.wait_ge(sem("x_loaded"), 32)
            for j in range(2):
                for d in range(4):
                    for t in range(TT):
                        r = rows[t]
                        mm = t_.transpose(quad(f"x{j}")[:, d, P * t:P * t + r],
                                          xrows[0:r, t, P * (4 * j + d):P * (4 * j + d + 1)],
                                          ident[0:r, 0:r])
                mm.then_inc(sem("x_turned"), 1)
            pe.wait_ge(sem("small_loaded"), 16 * 8)
            before_quad(pe, "vec")
            t_.transpose(quad("vec")[:, 0, 0:NV], vrows[:, :], ident[0:NV, 0:NV])
            for d in range(DT):
                mm = t_.transpose(quad("vec")[:, 1, 2 * B * d:2 * B * (d + 1)],
                                  brows[:, P * d:P * (d + 1)], ident[0:2 * B, 0:2 * B])
            mm.then_inc(sem("vec_turned"), 1)

            def sum_squares(which):
                if which != "final":
                    before_quad(pe, "ss_" + which)
                out = ss_bank(which)[:, 0:T]
                for j in range(2):
                    pe.wait_ge(sem("sq_" + which), j + 1)
                    for d in range(4 * j, 4 * j + 4):
                        mm = t_.matmul(out, ones[:, :], sq[:, d, :], start=(d == 0),
                                       stop=(d == DT - 1))
                mm.then_inc(sem("ss_done_" + which), 1)

            def three(out, w, lo, wslice, xhi, xlo, start, stop, **kw):
                t_.matmul(out, w[wslice], xhi, start=start, stop=False, **kw)
                t_.matmul(out, w[wslice], xlo, start=False, stop=False, **kw)
                return t_.matmul(out, lo[wslice], xhi, start=False, stop=stop, **kw)

            def project(n, name, ready):
                before_quad(pe, name)
                for half in range(2):
                    p = 2 * n + half
                    pe.wait_ge(lo_done, p + 1)
                    if ready:
                        pe.wait_ge(sem(ready), half + 1)
                    mm = project_half(p % SPLIT, half, quad(name))
                    mm.then_inc(used, 1)

            def project_half(buf, half, q):
                for j in range(4):
                    for k in range(4):
                        kt = 4 * half + k
                        c = k * FW + j * P
                        mm = three(q[:, j, 0:T], whi, wlo,
                                   (slice(None), buf, slice(c, c + P)), xh[:, kt, :], xl[:, kt, :],
                                   kt == 0, kt == DT - 1)
                return mm

            sum_squares("mix0")
            for c in range(8):
                project(C_IN + c, f"in{c}", "xl_mix0" if c == 0 else None)

            zq, zf, zv = z[:, 0:DT, :], z[:, DT:2 * DT, :], z[:, 2 * DT:3 * DT, :]
            for g in range(2):
                pe.wait_ge(sem("z_ready"), 6)
                pe.wait_ge(sem("k_in_ready"), 1)
                before_quad(pe, f"t{g}")
                for s, bank in ((zv, 0), (pb, 2)):
                    for b in range(BLK):
                        for h in range(4):
                            mm = t_.transpose(quad(f"t{g}")[:, bank + b, P * h:P * (h + 1)],
                                              s[:, 4 * g + h, P * b:P * (b + 1)], ident[:, :])
                mm.then_inc(sem(f"turned{g}"), 1)
                pe.wait_ge(sem("q2_ready"), 1) if g == 0 else None
                before_quad(pe, f"a{g}")
                for b in range(BLK):
                    for h in range(4):
                        tok = slice(P * b, P * (b + 1))
                        mm = t_.matmul(quad(f"a{g}")[:, b, P * h:P * (h + 1)],
                                       pb[:, 4 * g + h, tok], zq[:, 4 * g + h, tok],
                                       start=True, stop=True)
                mm.then_inc(sem(f"a_mm{g}"), 1)
                pe.wait_ge(sem("vtok_ready"), g + 1)
                pe.wait_ge(sem("ktok_ready"), g + 1)
                for b in range(BLK):
                    before_quad(pe, f"d{g}{b}")
                    for j in range(CPB):
                        s = slice(CH * j, CH * (j + 1))
                        for h in range(4):
                            mm = t_.matmul(quad(f"d{g}{b}")[:, j, P * h:P * (h + 1)],
                                           ktok[s, b, h, :], vtok[s, b, h, :],
                                           start=True, stop=True)
                    mm.then_inc(sem("d_mm"), 1)
                pe.wait_ge(sem("amask_ready"), g + 1)
                before_quad(pe, f"o{g}")
                for b in range(BLK):
                    for h in range(4):
                        t_.matmul(quad(f"o{g}")[:, b, P * h:P * (h + 1)], vtok[:, b, h, :],
                                  amask[:, b, h, :], start=(h == 0), stop=False,
                                  skip_group_check=True)
                for c in range(1, NC):
                    b, j = c // CPB, c % CPB
                    pe.wait_ge(sem("u_ready"), 4 * (g * NC + c))
                    for h in range(4):
                        mm = t_.matmul(
                            quad(f"o{g}")[:, b, P * h + CH * j:P * h + CH * (j + 1)],
                            U[:, c - 1, h, :], zf[:, 4 * g + h, CH * c:CH * (c + 1)],
                            start=False, stop=(c == NC - 1), skip_group_check=True)
                mm.then_inc(sem("o_mm"), 1)

            before_quad(pe, "ts")
            for s, bank in ((zv, 0), (kk, 2)):
                for h in range(DT):
                    mm = t_.transpose(quad("ts")[0:B, bank + h // 4, P * (h % 4):P * (h % 4 + 1)],
                                      s[:, h, TP:T], ident[:, :])
            mm.then_inc(sem("ts_turned"), 1)
            pe.wait_ge(sem("kv_rows2"), 1)
            before_quad(pe, "os")
            before_quad(pe, "outer")

            def outer(h):
                pe.wait_ge(sem("vbd_ready"), h + 1)
                if h >= 2:
                    pe.wait_ge(sem("state_new"), h - 1)
                for j in range(2):
                    mm = t_.matmul(quad("outer")[:, 2 * (h % 2) + j, :], ks[:, h, :],
                                   vbd[:, h % 2, 4 * j:4 * j + 4, :].rearrange("b c v -> b (c v)"),
                                   start=True, stop=True)
                mm.then_inc(sem("outer_mm"), 1)

            outer(0)
            for h in range(DT):
                if h + 1 < DT:
                    outer(h + 1)
                pe.wait_ge(sem("state_new"), h + 1)
                for b in range(B):
                    mm = t_.matmul(quad("os")[:, 0, B * h + b:B * h + b + 1], st[:, h % 2, b, :],
                                   zq[:, h, TP + b:TP + b + 1], start=True, stop=True)
                mm.then_inc(sem("state_read"), 1)
            for j in range(2):
                before_quad(pe, f"on{j}")
                pe.wait_ge(sem("osq"), j + 1)
                for h in range(4):
                    mm = t_.matmul(quad(f"on{j}")[:, h, 0:T], ones[:, :], pb[:, 4 * j + h, :],
                                   start=True, stop=True)
                mm.then_inc(sem(f"on_mm{j}"), 1)
            for c in range(2):
                project(C_OUT + c, f"out{c}", "xl_out" if c == 0 else None)
            sum_squares("ffn0")

            P0 = 2 * C_FFN

            def up(q, base, reg):
                for half in range(2):
                    p = base + half
                    if reg is None:
                        pe.wait_ge(lo_done, p + 1)
                        pe.wait_ge(sem("xl_ffn0"), half + 1)
                    else:
                        pe.wait_ge(lo_done, reg * 6 + (p + 1))
                    project_half(p % SPLIT, half, Q[q]).then_inc(used, 1)

            def down(base, b, reg):
                pe.wait_ge(lo_done, base + 2 if reg is None else reg * 6 + (base + 2))
                pe.wait_ge(sem("fl_ready"), b + 1)
                for j in range(2):
                    for d in range(4):
                        for k in range(4):
                            c = (k % 2) * D + (4 * j + d) * P
                            mm = three(Q[j][:, d, 0:T], whi, wlo,
                                       (slice(None), (base + k // 2) % SPLIT, slice(c, c + P)),
                                       fh[:, k, :], fl[:, k, :], k == 0, k == 3)
                    if j == 0:
                        mm.then_inc(sem("w2_half"), 1)
                        yield
                    else:
                        mm.then_inc(used, 2)

            up(0, P0, None)
            up(1, P0 + 2, None)
            with pe.Fori(0, FB - 1) as i:
                pe.wait_ge(sem("fs_ready"), i + 1)
                pe.wait_ge(sem("x_added"), i * 2 + 1)
                up(0, P0 + 4, i)
                pe.wait_ge(sem("fx_ready"), i + 1)
                pe.wait_ge(sem("x_added"), i * 2 + 2)
                up(1, P0 + 6, i)
                pe.wait_ge(sem("fs_ready"), i + 2)
                halves = down(P0 + 8, i, i)
                next(halves)
                pe.wait_ge(sem("fx_ready"), i + 2)
                for _ in halves:
                    pass
            pe.wait_ge(sem("x_added"), 2 * FB)
            for _ in down(P0 + 4 + 6 * (FB - 1), FB - 1, None):
                pass

            sum_squares("mix1")
            for c in range(6):
                project(C_CIN + c, f"cin{c}", "xl_mix1" if c == 0 else None)
            pe.wait_ge(sem("cg_ready"), 2)
            before_quad(pe, "cg")
            for d in range(DT):
                mm = t_.transpose(quad("cg")[0:2 + B, d // 4, P * (d % 4):P * (d % 4 + 1)],
                                  cg[:, d, :], ident[:, :])
            mm.then_inc(sem("cg_turned"), 1)
            for c in range(2):
                project(C_COUT + c, f"cout{c}", "xl_cout" if c == 0 else None)
            sum_squares("ffn1")
            pe.wait_ge(sem("xn_ffn1"), DT)
            before_quad(pe, "lg")
            for t in range(TT):
                r = rows[t]
                for d in range(DT):
                    mm = t_.matmul(quad("lg")[0:r, 0, E * t:E * (t + 1)],
                                   xn[:, d, P * t:P * t + r], router[:, d, :],
                                   start=(d == 0), stop=(d == DT - 1))
            mm.then_inc(sem("lg_mm"), 1)
            for t in range(2):
                before_quad(pe, f"xt{t}")
                turn_x(t_, t, rows).then_inc(sem("xt_turned"), 1)
            pe.wait_ge(sem("sel_ready"), 1)
            before_quad(pe, "rank")
            for u in range(TT + 1):
                out = quad("rank")[:, 0, E * u:E * (u + 1)]
                for s in range(min(u, TT)):
                    mm = t_.matmul(out, ones[:, :], sel[:, s, :], start=(s == 0),
                                   stop=(u == TT and s == TT - 1))
                if u < TT:
                    mm = t_.matmul(out, before[:, :], sel[:, u, :], start=(u == 0), stop=True)
            mm.then_inc(sem("rank_mm"), 1)
            before_quad(pe, "xt2")
            turn_x(t_, 2, rows).then_inc(sem("xt_turned"), 1)

            pe.wait_ge(sem("moe_ready"), 1)
            pe.wait_ge(sem("xtok_act"), 2)
            M0 = 2 * C_MOE

            def piece(k, q, reg):
                w = k * (2 * JOB) + (M0 + q + 1)
                pe.wait_ge(lo_done, w if reg is None else w + reg * 6)

            def up_m(bank, k, q, reg):
                for half in range(2):
                    piece(k, q + half, reg)
                    high, low = bufs(q + half)
                    for c in range(4):
                        kt = 4 * half + c
                        w = slice(FW * c, FW * (c + 1))
                        out = Q[0][:, bank, :]
                        t_.matmul(out, xgh[:, kt, :], high[:, w], start=(kt == 0), stop=False)
                        t_.matmul(out, xgh[:, kt, :], low[:, w], start=False, stop=False)
                        mm = t_.matmul(out, xgl[:, kt, :], high[:, w], start=False,
                                       stop=(kt == DT - 1))
                    mm.then_inc(used, 1)

            def gather(k):
                pe.wait_ge(sem("pm_ready"), k * (2 * TT) + TT)
                for d in range(DT):
                    for t in range(TT):
                        r = rows[t]
                        mm = t_.matmul(Q[1][:, 2 + d // 4, P * (d % 4):P * (d % 4 + 1)],
                                       xtok[0:r, t, P * d:P * (d + 1)], pm[0:r, t, :],
                                       start=(t == 0), stop=(t == TT - 1))
                mm.then_inc(sem("xg_mm"), 1)
                pe.wait_ge(sem("pm_ready"), k * (2 * TT) + 2 * TT)
                for t in range(TT):
                    r = rows[t]
                    mm = t_.transpose(Q[0][:, 3, P * t:P * t + r], pw[0:r, t, :], ident[0:r, 0:r])
                mm.then_inc(sem("pwt_mm"), 1)

            def scatter(k):
                pe.wait_ge(sem("y_act"), k + 1)
                pe.wait_ge(sem("y_dve"), k + 2)
                for d in range(DT):
                    if d >= 2:
                        pe.wait_ge(sem("x_scattered"), k * DT + (DT + d - 1))
                    t_.matmul(Q[1][:, 2 + d % 2, 0:T], ysb[:, P * d:P * (d + 1)], pwt[:, :],
                              start=True, stop=True).then_inc(sem("scatter_mm"), 1)

            def head(k, e, col):
                gather(k)
                pe.wait_ge(sem("xgl_ready"), k + 1)
                up_m(0, k, 0, None)

            def body(k, e, col, ahead):

                def turn(nth):
                    pe.wait_ge(sem("hx_ready"), nth + 2)
                    for c in range(4):
                        mm = t_.transpose(Q[0][:, 2, P * c:P * (c + 1)], hx[:, P * c:P * (c + 1)],
                                          ident[:, :])
                    mm.then_inc(sem("h_turned"), 1)

                def down_m(nth, q, reg, last):
                    pe.wait_ge(sem("htl_ready"), nth + 1)
                    for half in range(2):
                        piece(k, q + half, reg)
                        high, low = bufs(q + half)
                        for c in range(2):
                            f = 2 * half + c
                            for j in range(2):
                                w = slice(D * c + 512 * j, D * c + 512 * (j + 1))
                                out = Q[1][:, j, :]
                                for lhs, rhs in ((hth, high), (hth, low), (htl, high)):
                                    mm = t_.matmul(out, lhs[:, f, :], rhs[:, w], start=False,
                                                   stop=(last and f == 3 and lhs is htl),
                                                   skip_group_check=True)
                        mm.then_inc(used, 1)

                kb = k * FB
                up_m(1, k, 2, None)
                for j in range(2):
                    t_.matmul(Q[1][:, j, :], zero[:, 0:P], zero[:, :], start=True, stop=False,
                              skip_group_check=True)
                with pe.Fori(0, FB - 1) as i:
                    pe.wait_ge(sem("hs_ready"), kb + i + 1)
                    up_m(0, k, 4, i)
                    turn(kb + i)
                    up_m(1, k, 6, i)
                    down_m(kb + i, 8, i, False)
                turn(kb + (FB - 1))
                if ahead:
                    gather(k + 1)
                down_m(kb + (FB - 1), 4 + 6 * (FB - 1), None, True)
                if ahead:
                    pe.wait_ge(sem("xgl_ready"), k + 2)
                    up_m(0, k + 1, 0, None)
                pe.wait_ge(sem("pwt_ready"), k + 1)
                scatter(k)

            jobs(pe, head, body)
            sum_squares("final")
            pe.wait_ge(sem("xn_final"), DT)
            for t, (q, bank) in enumerate(((1, 0), (1, 2), (0, 0))):
                r = rows[t]
                for d in range(DT):
                    mm = t_.transpose(Q[q][0:r, bank + d // 4, P * (d % 4):P * (d % 4 + 1)],
                                      xn[:, d, P * t:P * t + r], ident[:, :])
                mm.then_inc(sem("y_turned"), 1)



_INS = ["x_prompt", "x_sample", "state_hgrn", "state_conv", "norm_mix", "norm_ffn", "norm_final",
        "hgrn_w_in", "hgrn_lb", "hgrn_g_norm", "hgrn_w_out", "conv_w_in", "conv_w", "conv_w_out",
        "ffn_w1", "ffn_w3", "ffn_w2", "moe_router", "moe_w1", "moe_w3", "moe_w2"]
_OUTS = [(1, 256, 1024), (8, 1, 1024), (1, 1, 8, 128, 128), (8, 1, 8, 128, 128), (1, 1, 2, 1024),
         (8, 1, 2, 1024)]


def kernel(**inputs):
    import numpy as _np
    import concourse.bacc as _bacc
    from concourse import mybir as _mybir
    from concourse.bass_utils import run_bass_kernel_spmd as _run

    nc = _bacc.Bacc("TRN2", target_bir_lowering=False, num_devices=1, dynamic_dma_scratch_size=1024)
    arrays, args = {}, []
    for name in _INS:
        a = _np.ascontiguousarray(inputs[name])
        arrays[f"in_{name}"] = a
        args.append(nc.dram_tensor(f"in_{name}", a.shape, _mybir.dt.from_np(a.dtype), kind="ExternalInput").ap())
    for i, shape in enumerate(_OUTS):
        args.append(nc.dram_tensor(f"out_{i}", shape, _mybir.dt.float32, kind="ExternalOutput").ap())
    build(nc, *args)
    r = _run(nc, [arrays], core_ids=[0])
    return tuple(r.results[0][f"out_{i}"] for i in range(len(_OUTS)))
```
